# Optimizing a Trainium2 kernel written in Bass

```python
import math
import jax, jax.numpy as jnp
from jax import lax
import numpy as np

D_MODEL = 1024
BATCH = 1
SEQ = 256
DEPTH = 2

N_MIXERS = 2
EPS = 1e-6
A_HEADS = 16
A_KV_HEADS = 4
A_HEAD_DIM = D_MODEL // A_HEADS
A_GROUP = A_HEADS // A_KV_HEADS
A_QKV_DIM = (A_HEADS + 2 * A_KV_HEADS) * A_HEAD_DIM
WINDOW = 128
ROPE_THETA = 10000.0
B_HEADS = 8
B_HEAD_DIM = D_MODEL // B_HEADS
B_KEY_DIM = B_HEADS * B_HEAD_DIM
B_IN_DIM = 4 * B_KEY_DIM + 2 * B_HEADS
CONV_WIDTH = 4
CHUNK = 64
D_FF = 3584
N_EXPERTS = 8
TOP_K = 2

kernel_name = "hybrid_swa_sink_gdn_moe"

def rms_norm(x, w):
    xf = x.astype(jnp.float32)
    y = xf * lax.rsqrt(jnp.mean(xf * xf, axis=-1, keepdims=True) + EPS)
    return (y * w.astype(jnp.float32)).astype(x.dtype)

def rope_tables(seq):
    inv = 1.0 / (ROPE_THETA ** (jnp.arange(0, A_HEAD_DIM, 2, dtype=jnp.float32) / A_HEAD_DIM))
    ang = jnp.arange(seq, dtype=jnp.float32)[:, None] * inv[None, :]
    return jnp.cos(ang), jnp.sin(ang)

def apply_rope(x, cos, sin):
    x1, x2 = jnp.split(x, 2, axis=-1)
    c = cos[None, :, None, :].astype(x.dtype)
    s = sin[None, :, None, :].astype(x.dtype)
    return jnp.concatenate([x1 * c - x2 * s, x2 * c + x1 * s], axis=-1)

def swa_sink_attention(h, w_qkv, b_qkv, sinks, w_o, cos, sin):
    B, T, _ = h.shape
    qkv = h @ w_qkv + b_qkv
    q, k, v = jnp.split(qkv, [A_HEADS * A_HEAD_DIM, (A_HEADS + A_KV_HEADS) * A_HEAD_DIM], axis=-1)
    q = apply_rope(q.reshape(B, T, A_HEADS, A_HEAD_DIM), cos, sin)
    k = apply_rope(k.reshape(B, T, A_KV_HEADS, A_HEAD_DIM), cos, sin)
    v = v.reshape(B, T, A_KV_HEADS, A_HEAD_DIM)
    nb = T // WINDOW
    qb = q.reshape(B, nb, WINDOW, A_KV_HEADS, A_GROUP, A_HEAD_DIM)

    def band(t):
        tb = t.reshape(B, nb, WINDOW, A_KV_HEADS, A_HEAD_DIM)
        prev = jnp.pad(tb[:, :-1], ((0, 0), (1, 0), (0, 0), (0, 0), (0, 0)))
        return jnp.concatenate([prev, tb], axis=2)

    kb, vb = band(k), band(v)
    scores = jnp.einsum('bnqhgd,bnkhd->bnhgqk', qb, kb).astype(jnp.float32) * (A_HEAD_DIM ** -0.5)
    qi = jnp.arange(WINDOW)[:, None]
    kj = jnp.arange(2 * WINDOW)[None, :]
    rel = WINDOW + qi - kj
    in_band = (rel >= 0) & (rel < WINDOW)
    blk = jnp.arange(nb)[:, None, None]
    valid = in_band[None] & ((blk > 0) | (kj[None] >= WINDOW))
    scores = jnp.where(valid[None, :, None, None], scores, -jnp.inf)
    sink = jnp.broadcast_to(sinks.astype(jnp.float32).reshape(1, 1, A_KV_HEADS, A_GROUP, 1, 1),
                            scores.shape[:-1] + (1,))
    probs = jax.nn.softmax(jnp.concatenate([scores, sink], axis=-1), axis=-1)[..., :-1]
    o = jnp.einsum('bnhgqk,bnkhd->bnqhgd', probs.astype(vb.dtype), vb)
    return o.reshape(B, T, A_HEADS * A_HEAD_DIM) @ w_o

def causal_depthwise_conv(x, w):
    C = x.shape[-1]
    return lax.conv_general_dilated(x, w[:, None, :].astype(x.dtype), window_strides=(1,),
                                    padding=[(CONV_WIDTH - 1, 0)],
                                    dimension_numbers=('NWC', 'WIO', 'NWC'),
                                    feature_group_count=C)

def l2_normalize(x):
    return x * lax.rsqrt(jnp.sum(x * x, axis=-1, keepdims=True) + EPS)

def chunked_gated_delta_rule(q, k, v, g, beta):
    B, T, H, D = q.shape
    n = T // CHUNK

    def chunks(t):
        return jnp.moveaxis(t.reshape((B, n, CHUNK) + t.shape[2:]), 3, 2)

    qc = chunks(q * (D ** -0.5))
    kc, vc = chunks(k), chunks(v)
    gc = jnp.cumsum(chunks(g), axis=-1)
    bc = chunks(beta)
    idx = jnp.arange(CHUNK)
    causal = idx[:, None] >= idx[None, :]
    strict = idx[:, None] > idx[None, :]
    decay = jnp.exp(jnp.where(causal, gc[..., :, None] - gc[..., None, :], -jnp.inf))
    kb = kc * bc[..., None]
    lower = jnp.where(strict, jnp.einsum('bnhid,bnhjd->bnhij', kb, kc) * decay, 0.0)
    eye = jnp.eye(CHUNK, dtype=jnp.float32)
    rhs = jnp.concatenate([vc * bc[..., None], kb * jnp.exp(gc)[..., None]], axis=-1)
    sol = lax.linalg.triangular_solve(eye + lower, rhs, left_side=True, lower=True)
    u, w = jnp.split(sol, 2, axis=-1)
    intra = jnp.einsum('bnhid,bnhjd->bnhij', qc, kc) * decay

    def step(S, inp):
        q_i, k_i, u_i, w_i, g_i, a_i = inp
        v_new = u_i - jnp.einsum('bhcd,bhde->bhce', w_i, S)
        o = (jnp.einsum('bhcd,bhde->bhce', q_i * jnp.exp(g_i)[..., None], S)
             + jnp.einsum('bhij,bhje->bhie', a_i, v_new))
        g_last = g_i[..., -1:]
        S = (S * jnp.exp(g_last)[..., None]
             + jnp.einsum('bhcd,bhce->bhde', k_i * jnp.exp(g_last - g_i)[..., None], v_new))
        return S, o

    xs = tuple(jnp.moveaxis(t, 1, 0) for t in (qc, kc, u, w, gc, intra))
    S0 = jnp.zeros((B, H, D, D), jnp.float32)
    _, o = lax.scan(step, S0, xs)
    o = jnp.swapaxes(jnp.moveaxis(o, 0, 1), 2, 3)
    return o.reshape(B, T, H, D)

def gated_deltanet(h, w_in, conv_w, a_log, dt_bias, o_norm, w_o):
    B, T, _ = h.shape
    proj = h @ w_in
    qkv, z, b, a = jnp.split(proj, [3 * B_KEY_DIM, 4 * B_KEY_DIM, 4 * B_KEY_DIM + B_HEADS], axis=-1)
    qkv = jax.nn.silu(causal_depthwise_conv(qkv, conv_w))
    q, k, v = [t.reshape(B, T, B_HEADS, B_HEAD_DIM).astype(jnp.float32) for t in jnp.split(qkv, 3, axis=-1)]
    q, k = l2_normalize(q), l2_normalize(k)
    beta = jax.nn.sigmoid(b.astype(jnp.float32))
    g = -jnp.exp(a_log.astype(jnp.float32)) * jax.nn.softplus(a.astype(jnp.float32) + dt_bias.astype(jnp.float32))
    o = chunked_gated_delta_rule(q, k, v, g, beta)
    o = rms_norm(o, o_norm) * jax.nn.silu(z.reshape(B, T, B_HEADS, B_HEAD_DIM).astype(jnp.float32))
    return o.reshape(B, T, B_KEY_DIM).astype(h.dtype) @ w_o

def swiglu(h, w_gate, w_up, w_down):
    return (jax.nn.silu(h @ w_gate) * (h @ w_up)) @ w_down

def moe_swiglu(h, w_router, w_gate, w_up, w_down):
    B, T, D = h.shape
    ht = h.reshape(B * T, D)
    logits = (ht @ w_router).astype(jnp.float32)
    top_logits, top_idx = lax.top_k(logits, TOP_K)
    top_w = jax.nn.softmax(top_logits, axis=-1)
    combine = jnp.sum(jax.nn.one_hot(top_idx, N_EXPERTS, dtype=jnp.float32) * top_w[..., None], axis=1)
    out = jnp.zeros_like(ht)
    for e in range(N_EXPERTS):
        y = swiglu(ht, w_gate[e], w_up[e], w_down[e])
        out = out + combine[:, e:e + 1].astype(ht.dtype) * y
    return out.reshape(B, T, D)

def setup_inputs(seed: int = 0) -> dict:
    key = jax.random.key(seed)
    ks = iter(jax.random.split(key, 32))
    n_a = (DEPTH + 1) // 2
    n_b = DEPTH // 2

    def normal(shape, scale):
        return jax.random.normal(next(ks), shape, jnp.float32) * scale

    def gain(shape):
        return 1.0 + 0.02 * jax.random.normal(next(ks), shape, jnp.float32)

    x = jax.random.normal(next(ks), (BATCH, SEQ, D_MODEL), jnp.float32)
    dt = jnp.exp(jax.random.uniform(next(ks), (n_b, B_HEADS), jnp.float32, math.log(1e-3), math.log(1e-1)))
    dt_bias = dt + jnp.log(-jnp.expm1(-dt))
    a_log = jnp.log(jax.random.uniform(next(ks), (n_b, B_HEADS), jnp.float32, 1.0, 16.0))
    return {
        'x': x,
        'a_norm': gain((n_a, D_MODEL)),
        'a_w_qkv': normal((n_a, D_MODEL, A_QKV_DIM), D_MODEL ** -0.5),
        'a_b_qkv': normal((n_a, A_QKV_DIM), 0.02),
        'a_sinks': normal((n_a, A_HEADS), 1.0),
        'a_w_o': normal((n_a, A_HEADS * A_HEAD_DIM, D_MODEL), (A_HEADS * A_HEAD_DIM) ** -0.5),
        'f_norm': gain((n_a, D_MODEL)),
        'f_w_gate': normal((n_a, D_MODEL, D_FF), D_MODEL ** -0.5),
        'f_w_up': normal((n_a, D_MODEL, D_FF), D_MODEL ** -0.5),
        'f_w_down': normal((n_a, D_FF, D_MODEL), D_FF ** -0.5),
        'b_norm': gain((n_b, D_MODEL)),
        'b_w_in': normal((n_b, D_MODEL, B_IN_DIM), D_MODEL ** -0.5),
        'b_conv_w': normal((n_b, CONV_WIDTH, 3 * B_KEY_DIM), CONV_WIDTH ** -0.5),
        'b_a_log': a_log,
        'b_dt_bias': dt_bias,
        'b_o_norm': gain((n_b, B_HEAD_DIM)),
        'b_w_o': normal((n_b, B_KEY_DIM, D_MODEL), B_KEY_DIM ** -0.5),
        'm_norm': gain((n_b, D_MODEL)),
        'm_w_router': normal((n_b, D_MODEL, N_EXPERTS), D_MODEL ** -0.5),
        'm_w_gate': normal((n_b, N_EXPERTS, D_MODEL, D_FF), D_MODEL ** -0.5),
        'm_w_up': normal((n_b, N_EXPERTS, D_MODEL, D_FF), D_MODEL ** -0.5),
        'm_w_down': normal((n_b, N_EXPERTS, D_FF, D_MODEL), D_FF ** -0.5),
        'final_norm': gain((D_MODEL,)),
    }

def reference(x, a_norm, a_w_qkv, a_b_qkv, a_sinks, a_w_o, f_norm, f_w_gate, f_w_up, f_w_down,
              b_norm, b_w_in, b_conv_w, b_a_log, b_dt_bias, b_o_norm, b_w_o,
              m_norm, m_w_router, m_w_gate, m_w_up, m_w_down, final_norm):
    cos, sin = rope_tables(x.shape[1])
    h = x
    for layer in range(DEPTH):
        j = layer // N_MIXERS
        if layer % N_MIXERS == 0:
            h = h + swa_sink_attention(rms_norm(h, a_norm[j]), a_w_qkv[j], a_b_qkv[j], a_sinks[j], a_w_o[j], cos, sin)
            h = h + swiglu(rms_norm(h, f_norm[j]), f_w_gate[j], f_w_up[j], f_w_down[j])
        else:
            h = h + gated_deltanet(rms_norm(h, b_norm[j]), b_w_in[j], b_conv_w[j], b_a_log[j], b_dt_bias[j], b_o_norm[j], b_w_o[j])
            h = h + moe_swiglu(rms_norm(h, m_norm[j]), m_w_router[j], m_w_gate[j], m_w_up[j], m_w_down[j])
    return rms_norm(h, final_norm)


_drawn_inputs = setup_inputs


def setup_inputs(seed=0):
    import zlib

    import numpy as np

    out = dict(_drawn_inputs(seed))
    spreads = {}
    factors = {}
    for name, (base, spread) in spreads.items():
        noise = np.random.default_rng([zlib.crc32(name.encode()), seed]).standard_normal(out[name].shape)
        drawn = base * np.exp(spread * noise) if base else spread * noise
        out[name] = __import__('jax').numpy.asarray(drawn.astype(out[name].dtype))
    for name, factor in factors.items():
        out[name] = (out[name] * factor).astype(out[name].dtype)
    return out
```

```python
import concourse.bass as bass
from concourse import mybir
from contextlib import ExitStack
import numpy as np

D = 1024
T = 256
TT = T // 128
KD = D // 128
F = 3584
CH = 512
NC = F // CH
E = 8
AH, AKV, AD = 16, 4, 64
AG = AH // AKV
QKV = (AH + 2 * AKV) * AD
WINDOW = 128
BH, BD = 8, 128
TAPS = 4
CHUNK = 64
EPS = 1e-6
NEG = -1e30
LEVELS = 6
RAW = 6
SPLIT = 3
SUB = 2048
SUBS_FFN = 6 * NC
JOBS = 11

CONST = {}
_at = 0
for _n, _w in (("ident", 128), ("att", 256), ("tri", 128), ("same", 128), ("first", 128), ("second", 128),
               ("mask_l", 128), ("mask_t", 128), ("levels", 128 * LEVELS), ("before", 128), ("ones", 128),
               ("iota", 256), ("cos", 64), ("sin", 64)):
    CONST[_n] = (_at, _at + _w)
    _at += _w
NCONST = _at


def constants():
    c = np.zeros((128, NCONST), np.float32)

    def put(name, value):
        c[:, CONST[name][0]:CONST[name][1]] = np.asarray(value, np.float32).reshape(128, -1)

    i, j = np.arange(128)[:, None], np.arange(128)[None, :]
    same = i // CHUNK == j // CHUNK
    put("ident", i == j)
    rel = WINDOW + i - np.arange(2 * WINDOW)[None, :]
    put("att", np.where((rel >= 0) & (rel < WINDOW), 0.0, NEG))
    put("tri", same & (i <= j))
    put("same", same)
    put("first", np.broadcast_to(i < CHUNK, (128, 128)))
    put("second", np.broadcast_to(i >= CHUNK, (128, 128)))
    put("mask_l", np.where(same & (i > j), 0.0, NEG))
    put("mask_t", np.where(same & (i <= j), 0.0, NEG))
    levels = [(i // (2 << l) == j // (2 << l)) & (i // (1 << l) > j // (1 << l)) for l in range(LEVELS)]
    put("levels", np.stack(levels, 1))
    put("before", i < j)
    put("ones", np.ones((128, 128)))
    put("iota", np.broadcast_to(np.arange(256)[None, :], (128, 256)))
    inv = 1.0 / (np.float32(10000.0) ** (np.arange(0, AD, 2, dtype=np.float32) / AD))
    ang = (np.arange(T, dtype=np.float32)[:, None] * inv[None, :]).astype(np.float32)
    put("cos", np.cos(ang).reshape(TT, 128, 32).transpose(1, 0, 2))
    put("sin", np.sin(ang).reshape(TT, 128, 32).transpose(1, 0, 2))
    return c


def hybrid_kernel(nc, x, a_norm, a_w_qkv, a_b_qkv, a_sinks, a_w_o, f_norm, f_w_gate, f_w_up, f_w_down,
                  b_norm, b_w_in, b_conv_w, b_a_log, b_dt_bias, b_o_norm, b_w_o,
                  m_norm, m_w_router, m_w_gate, m_w_up, m_w_down, final_norm, consts, out,
                  stages=("att", "ffn", "gdn", "moe")):
    f32, f32r = mybir.dt.float32, mybir.dt.float32r
    i32, u32 = mybir.dt.int32, mybir.dt.uint32
    ALU, ACT, AX = mybir.AluOpType, mybir.ActivationFunctionType, mybir.AxisListType
    ds = bass.ds

    base, at = {}, 0
    for name, n in (("att", 10), ("ffn", SUBS_FFN), ("gdn", 20), ("moe", 0)):
        base[name] = at
        at += n if name in stages else 0

    with ExitStack() as ctx:
        def sb(name, shape, dt=f32, c=ctx):
            return c.enter_context(nc.sbuf_tensor(name, shape, dt))

        sems = {}

        def sem(name):
            if name not in sems:
                sems[name] = ctx.enter_context(nc.semaphore(name))
            return sems[name]

        with ExitStack() as c:
            def t8(name):
                return sb(name, [128, BH, 128], c=c)
            decay, decayT, low, lowM, inv, invT, yT, attnT, vbeta, kbeta, u_sol, wT = map(
                t8, ("decay", "decayT", "low", "lowM", "inv", "invT", "yT", "attnT", "vbeta", "kbeta", "u_sol", "wT"))
        WH = sb("w_high", [128, SPLIT, SUB], f32r)
        WL = sb("w_low", [128, SPLIT, SUB], f32r)
        W = sb("w_raw", [128, RAW, SUB])
        h = sb("h", [128, TT, D])
        xs = sb("xs", [128, TT, D])
        xH = sb("x_high", [128, KD, T], f32r)
        xL = sb("x_low", [128, KD, T], f32r)
        cst = sb("cst", [128, NCONST])
        rows = sb("rows", [128, 128])
        cols = sb("cols", [128, 128])
        w_fin = sb("w_fin", [128, D])
        ss = sb("ss", [128, 5, TT])
        ms = sb("ms", [128, 5, TT])
        rstd = sb("rstd", [128, 5, TT])
        neg_half = sb("neg_half", [128, 32])
        small_w = sb("small_w", [128, KD, 16 + E])
        swH = sb("sw_high", [128, KD, 16 + E], f32r)
        swL = sb("sw_low", [128, KD, 16 + E], f32r)

        with ExitStack() as c:
            bias = sb("bias", [128, QKV], c=c)
            sinks = sb("sinks", [128, AH], c=c)
            qkv = sb("qkv", [128, TT, QKV], c=c)
            rot = sb("rot", [128, TT, (AH + 2 * AKV) * AD], c=c)
            qkT = sb("qkT", [128, 12, T], c=c)
            prob = sb("prob", [128, 2, AG, 256], c=c)
            probT = sb("probT", [128, 2, 2 * AG, 128], c=c)
            mx = sb("mx", [128, 8, AG], c=c)
            negm = sb("negm", [128, 8, AG], c=c)
            sink_e = sb("sink_e", [128, 8, AG], c=c)
            den = sb("den", [128, 8, AG], c=c)
            rden = sb("rden", [128, 8, AG], c=c)
        ropeA = prob[:].rearrange("p a h k -> p (a h k)")[:, 0:1280]
        ropeB = probT[:].rearrange("p a h k -> p (a h k)")[:, 0:1280]
        o_att = xs

        with ExitStack() as c:
            fg = sb("f_gate", [128, TT, CH], c=c)
            fa = sb("f_act", [128, TT, CH], c=c)
            faH = sb("f_act_high", [128, TT, 4, 128], f32r, c=c)
            faL = sb("f_act_low", [128, TT, 4, 128], f32r, c=c)

        with ExitStack() as c:
            with ExitStack() as c2:
                qT, kT, qgT = (sb(n, [128, BH, 128], c=c2) for n in ("qT", "kT", "qgT"))
                state = [sb(n, [128, BH, BD], c=c2) for n in ("state0", "state1")]
                v_new = sb("v_new", [128, BH, BD], c=c2)
            cv = sb("cv", [128, 24, T], c=c)
            tok = sb("tok", [128, 3, TT, BH, BD], c=c)
            z = sb("z", [128, TT, D], c=c)
            o_w = sb("o_w", [128, BD], c=c)
            hpar = sb("hpar", [128, 2, BH], c=c)
            HS = [128, TT, BH]
            (ba_b, ba_a, t_a, t_b, beta, gate, gcum, egc, kdec, bgc, sso, rso) = (
                sb(n, HS, c=c) for n in ("ba_b", "ba_a", "t_a", "t_b", "beta", "gate", "gcum", "egc",
                                         "kdec", "bgc", "sso", "rso"))
            nega = sb("nega", [128, BH], c=c)
            egl = sb("egl", [128, 2, TT, BH], c=c)
            ssq = sb("ssq", [128, 2, TT, BH], c=c)
            rq = sb("rq", [128, 2, TT, BH], c=c)
        q_tok, k_tok, v_tok = tok[:, 0], tok[:, 1], tok[:, 2]

        with ExitStack() as c:
            xsH = sb("xs_high", [128, TT, D], f32r, c=c)
            xsL = sb("xs_low", [128, TT, D], f32r, c=c)
            ysH = sb("ys_high", [128, D], f32r, c=c)
            ysL = sb("ys_low", [128, D], f32r, c=c)
            mg = sb("m_gate", [128, CH], c=c)
            ma = sb("m_act", [128, CH], c=c)
            maH = sb("m_act_high", [128, 4, 128], f32r, c=c)
            maL = sb("m_act_low", [128, 4, 128], f32r, c=c)
            pick = sb("pick", [128, TT, 128], f32r, c=c)
            pickT = sb("pickT", [128, TT, 128], f32r, c=c)
            identR = sb("identR", [128, 128], f32r, c=c)
            R8 = [128, TT, E]
            lg, top, sel0, sel1, sel, cw, key = (
                sb(n, R8, c=c) for n in ("lg", "top", "sel0", "sel1", "sel", "cw", "key"))
            topi = sb("topi", R8, u32, c=c)
            topf = sb("topf", R8, c=c)
            w0, w1, gap = (sb(n, [128, TT], c=c) for n in ("w0", "w1", "gap"))
            cnt, over, opos, hit = (sb(n, [128, E], c=c) for n in ("cnt", "over", "opos", "hit"))
            jobf = sb("jobf", [128, 16], c=c)
            jobs = sb("jobs", [128, 16], i32, c=c)
            fin = sb("fin", [128, TT, D], c=c)
        NJ = 15
        LOADS = 3

        PS = ctx.enter_context(nc.psum_tensor("PS", [128, 8, 512], f32))

        def C(name):
            return cst[:, CONST[name][0]:CONST[name][1]]

        ident = C("ident")
        level = C("levels").rearrange("p (l j) -> p l j", l=LEVELS)

        def over_heads(ap, n):
            return ap.unsqueeze(1).broadcast_to([128, n, ap.shape[-1]])

        def per_head(ap, w):
            return ap.unsqueeze(2).broadcast_to([128, ap.shape[-1], w])

        w_in = [sem(f"w_in{i}") for i in range(RAW)]
        hi_done, lo_done = sem("hi_done"), sem("lo_done")
        w_used = sem("w_used")
        loaded = sem("loaded")
        loaded_att, loaded_gdn = sem("loaded_att"), sem("loaded_gdn")
        h_done = sem("h_done")
        ss_done, rstd_done, xs_done = sem("ss_done"), sem("rstd_done"), sem("xs_done")
        xt_ps, xh_done, xl_done = sem("xt_ps"), sem("xh_done"), sem("xl_done")

        norm_no, turn_no, seq_n, seq_t = {}, {}, 0, 0
        for st, norms, turns in (("att", ["att"], ["att", "att_o"]), ("ffn", ["ffn"], ["ffn"]),
                                 ("gdn", ["gdn"], ["gdn", "gdn_o"]), ("moe", ["moe"], ["moe"])):
            if st in stages:
                for n in norms:
                    norm_no[n] = seq_n
                    seq_n += 1
                for n in turns:
                    turn_no[n] = seq_t
                    seq_t += 1
        norm_no["fin"] = seq_n
        stage_no = {s: i for i, s in enumerate(stages)}
        NORM_COL = {"att": 0, "ffn": 1, "gdn": 2, "moe": 3}

        def raw_view(slot, kind):
            if kind == "cols":
                return W[:, slot, :].rearrange("p (k c) -> p k c", k=4)
            return W[:, slot, :].rearrange("p (f c) -> p f c", f=2)

        def fetch(sp, n, r, kind, src):
            if n >= RAW:
                sp.wait_ge(lo_done, n - RAW + 1 + r * RAW)
            sp.dma_start(raw_view(n % RAW, kind), src).then_inc(w_in[n % RAW], 16)

        def split_high(act, n, r=0):
            act.wait_ge(w_in[n % RAW], 16 * (n // RAW + 1) + r * 16)
            if n >= SPLIT:
                act.wait_ge(w_used, n - SPLIT + 1 + r * RAW)
            nc.scalar.activation(WH[:, n % SPLIT, :], W[:, n % RAW, :], ACT.Copy).then_inc(hi_done, 1)

        def split_low(dve, n, r=0):
            dve.wait_ge(hi_done, n + 1 + r * RAW)
            nc.vector.tensor_tensor(WL[:, n % SPLIT, :], W[:, n % RAW, :], WH[:, n % SPLIT, :].bitcast(f32),
                                    ALU.subtract).then_inc(lo_done, 1)

        def high_low(n, blocks):
            w = "p (k c) -> p k c"
            return (WH[:, n % SPLIT, :].rearrange(w, k=blocks), WL[:, n % SPLIT, :].rearrange(w, k=blocks))

        def mm3(o, sH, sL, mH, mL, first, last):
            nc.tensor.matmul(o, sH, mH, start=first, stop=False)
            nc.tensor.matmul(o, sH, mL, start=False, stop=False)
            return nc.tensor.matmul(o, sL, mH, start=False, stop=last)

        def col_src(w, cb, half):
            return w.rearrange("(k p) c -> p k c", p=128)[:, 4 * half:4 * half + 4, cb * CH:(cb + 1) * CH]

        block = ctx.enter_context(nc.Block())

        @block.sync
        def _(sp):
            def fetch_cols(n, w, blocks):
                for cb in range(blocks):
                    for half in range(2):
                        fetch(sp, n, 0, "cols", col_src(w, cb, half))
                        n += 1

            def ffn_stream(n0, r0, gate, up, down, loop_r):
                g = gate.rearrange("a (k p) c -> p (a k) c", p=128)
                u = up.rearrange("a (k p) c -> p (a k) c", p=128)
                d = down.rearrange("a (f p) c -> p (a f) c", p=128)

                def block_of(w, half, c):
                    if isinstance(c, int):
                        return w[:, 4 * half:4 * half + 4, c * CH:(c + 1) * CH]
                    return w[:, 4 * half:4 * half + 4, ds(c * CH, CH)]

                for i, (w, half) in enumerate(((g, 0), (g, 1), (u, 0), (u, 1))):
                    fetch(sp, n0 + i, r0, "cols", block_of(w, half, 0))
                with sp.Fori(0, NC - 1) as i:
                    r = loop_r(i)
                    for k, (w, half) in enumerate(((g, 0), (g, 1), (u, 0), (u, 1))):
                        fetch(sp, n0 + 4 + k, r, "cols", block_of(w, half, i + 1))
                    for half in range(2):
                        fetch(sp, n0 + 8 + half, r, "rows", d[:, ds(4 * i + 2 * half, 2), :])
                for half in range(2):
                    fetch(sp, n0 + SUBS_FFN - 2 + half, r0, "rows", d[:, 4 * (NC - 1) + 2 * half:4 * (NC - 1) + 2 * half + 2, :])

            x_v = x[0].rearrange("(t p) d -> p t d", p=128)
            for t in range(TT):
                sp.dma_start(h[:, t], x_v[:, t]).then_inc(sem(f"x_in{t}"), 16)
            sp.dma_start(cst[:, 0:128], consts[:, 0:128]).then_inc(sem("ident_in"), 16)
            if "att" in stages:
                fetch_cols(base["att"], a_w_qkv[0], 2)
                sp.dma_start(cst[:, 128:], consts[:, 128:]).then_inc(sem("cst_in"), 16)
                fetch(sp, base["att"] + 4, 0, "cols", col_src(a_w_qkv[0], 2, 0))
                fetch(sp, base["att"] + 5, 0, "cols", col_src(a_w_qkv[0], 2, 1))
                fetch_cols(base["att"] + 6, a_w_o[0], D // CH)
            if "ffn" in stages:
                ffn_stream(base["ffn"], 0, f_w_gate, f_w_up, f_w_down, lambda i: i)
            if "gdn" in stages:
                fetch_cols(base["gdn"], b_w_in[0], 8)
                fetch_cols(base["gdn"] + 16, b_w_o[0], D // CH)
            if "moe" in stages:
                def job(j, e):
                    ffn_stream(base["moe"], j * NC, m_w_gate[0, ds(e, 1)], m_w_up[0, ds(e, 1)], m_w_down[0, ds(e, 1)],
                               lambda i: j * NC + i)

                with sp.Fori(0, E) as j:
                    job(j, j)
                sp.wait_ge(sem("jobs_done"), 1)
                njobs = sp.value_load(jobs[0:1, NJ:NJ + 1], min_val=E, max_val=JOBS)
                with sp.Fori(E, JOBS) as j:
                    with sp.If(j < njobs):
                        e = sp.value_load(jobs[0:1, ds(j + 1, 1)], min_val=0, max_val=E - 1)
                        job(j, e)
            out_v = out[0].rearrange("(t p) d -> p t d", p=128)
            for t in range(TT):
                sp.wait_ge(sem("fin_done"), t + 1)
                sp.dma_start(out_v[:, t], fin[:, t]).then_inc(sem("stored"), 16)
            sp.wait_ge(sem("stored"), 16 * TT)

        @block.gpsimd
        def _(pool):
            links = [0]

            def link(ins):
                links[0] += 1
                ins.then_inc(sem("pool_link"), 1)
                pool.wait_ge(sem("pool_link"), links[0])

            link(nc.gpsimd.memset(neg_half[:], -0.5))

            def norm(name):
                n = norm_no[name]
                for t in range(TT):
                    s = slice(t, t + 1)
                    pool.wait_ge(ss_done, TT * n + t + 1)
                    link(nc.gpsimd.tensor_scalar(ms[:, n, s], ss[:, n, s], 1.0 / D, EPS, ALU.mult, ALU.add))
                    nc.gpsimd.tensor_tensor(rstd[:, n, s], ms[:, n, s], neg_half[:, s], ALU.pow).then_inc(rstd_done, 1)

            for st in ("att", "ffn", "gdn", "moe"):
                if st not in stages:
                    continue
                norm(st)
                if st != "gdn":
                    continue
                flat = "p a t h -> p (a t h)"
                pool.wait_ge(sem("ssq_done"), 8)
                link(nc.gpsimd.tensor_scalar(ssq[:].rearrange(flat), ssq[:].rearrange(flat), EPS, None, ALU.add))
                link(nc.gpsimd.tensor_tensor(rq[:].rearrange(flat), ssq[:].rearrange(flat), neg_half[:, 0:32], ALU.pow))
                nc.gpsimd.tensor_scalar(rq[:, 0].rearrange("p t h -> p (t h)"), rq[:, 0].rearrange("p t h -> p (t h)"),
                                        BD ** -0.5, None, ALU.mult).then_inc(sem("rq_done"), 1)
                for t in range(TT):
                    pool.wait_ge(sem("low_done"), t + 1)
                    for l in range(1, LEVELS):
                        if l >= 2:
                            pool.wait_ge(sem("y_ps"), 2 * ((LEVELS - 1) * t + l - 1))
                        nc.gpsimd.tensor_tensor(lowM[:], low[:], over_heads(level[:, l], BH), ALU.mult)\
                            .then_inc(sem("lowM_done"), 1)
                    pool.wait_ge(sem("sso_done"), t + 1)
                    link(nc.gpsimd.tensor_scalar(sso[:, t], sso[:, t], 1.0 / BD, EPS, ALU.mult, ALU.add))
                    nc.gpsimd.tensor_tensor(rso[:, t], sso[:, t], neg_half[:, 0:BH], ALU.pow).then_inc(sem("rso_done"), 1)
            norm("fin")

        @block.scalar
        def _(act):
            links = [0]

            def link(ins):
                links[0] += 1
                ins.then_inc(sem("act_link"), 1)
                act.wait_ge(sem("act_link"), links[0])

            def bcast(v):
                return v.partition_broadcast(128)

            for dst, src in ((rows[0:8, :], a_norm[0].rearrange("(k p) -> k p", p=128)),
                             (rows[8:16, :], f_norm[0].rearrange("(k p) -> k p", p=128)),
                             (rows[16:24, :], b_norm[0].rearrange("(k p) -> k p", p=128)),
                             (rows[24:32, :], m_norm[0].rearrange("(k p) -> k p", p=128)),
                             (rows[32:128, :], b_conv_w[0].rearrange("j (f p) -> (j f) p", p=128)),
                             (w_fin[:], bcast(final_norm)),
                             (small_w[:, :, 0:16], b_w_in[0].rearrange("(k p) c -> p k c", p=128)[:, :, 4096:4112]),
                             (small_w[:, :, 16:16 + E], m_w_router[0].rearrange("(k p) c -> p k c", p=128))):
                act.dma_start(dst, src).then_inc(sem("rows_in") if dst.shape[0] < 128 else loaded, 16)
            if "att" in stages:
                act.dma_start(bias[:], bcast(a_b_qkv[0])).then_inc(loaded_att, 16)
                act.dma_start(sinks[:], bcast(a_sinks[0])).then_inc(loaded_att, 16)
            def small_high():
                act.wait_ge(loaded, 16 * LOADS)
                nc.scalar.activation(swH[:], small_w[:], ACT.Copy).then_inc(sem("swH_done"), 1)

            def norm(name):
                n = norm_no[name]
                for t in range(TT):
                    if n:
                        act.wait_ge(h_done, TT * (n - 1) + t + 1)
                    else:
                        act.wait_ge(sem(f"x_in{t}"), 16)
                    nc.scalar.activation(xs[:, t], h[:, t], ACT.Square, accum_out=ss[:, n, t:t + 1]).then_inc(ss_done, 1)

            def turn(name, scaled):
                m = turn_no[name]
                if m == 0:
                    act.wait_ge(sem("cols_done"), 1)
                for b in range(4):
                    act.wait_ge(xt_ps, 4 * m + b + 1)
                    for kk in range(2):
                        k = 2 * b + kk
                        scale = cols[:, 8 * NORM_COL[name] + k:8 * NORM_COL[name] + k + 1] if scaled else 1.0
                        last = nc.scalar.activation(xH[:, k, :], PS[:, 4 + b, 256 * kk:256 * kk + 256], ACT.Copy, scale=scale)
                    last.then_inc(xh_done, 1)

            def attention(n0):
                norm("att")
                for n in range(3):
                    split_high(act, n0 + n)
                turn("att", True)
                small_high()
                for n in range(3, 6):
                    split_high(act, n0 + n)
                for g in range(6):
                    if g == 2:
                        for n in range(6, 9):
                            split_high(act, n0 + n)
                    act.wait_ge(sem("qkT_ps"), g + 1)
                    nc.scalar.activation(qkT[:, 2 * g:2 * g + 2, :], PS[:, 4 + g % 4, :].rearrange("p (b c) -> p b c", b=2),
                                         ACT.Copy).then_inc(sem("qkT_done"), 1)
                for a in range(8):
                    t, nk = a % 2, 128 * (a % 2 + 1)
                    act.wait_ge(sem("masked"), a + 1)
                    for hh in range(AG):
                        last = nc.scalar.activation(prob[:, a % 2, hh, 0:nk], prob[:, a % 2, hh, 0:nk], ACT.Exp,
                                                    bias=negm[:, a, hh:hh + 1], accum_out=den[:, a, hh:hh + 1])
                    last = nc.scalar.activation(sink_e[:, a], sink_e[:, a], ACT.Exp)
                    last.then_inc(sem("exp_done"), 1)
                    act.wait_ge(sem("probT_ps"), a + 1)
                    if a >= 2:
                        act.wait_ge(sem("pv_ps"), a - 1)
                    nc.scalar.activation(probT[:, a % 2, 0:AG * (t + 1), :],
                                         PS[:, 4:5 + t, :].rearrange("p b (n q) -> p (b n) q", q=128), ACT.Copy)\
                        .then_inc(sem("probT_done"), 1)
                turn("att_o", False)
                split_high(act, n0 + 9)

            def ffn(n0):
                split_high(act, n0)
                split_high(act, n0 + 1)
                norm("ffn")
                turn("ffn", True)
                split_high(act, n0 + 2)
                split_high(act, n0 + 3)

                def silu(n, r):
                    act.wait_ge(w_used, n + r * RAW)
                    for t in range(TT):
                        nc.scalar.activation(fg[:, t], PS[:, t, :], ACT.Silu).then_inc(sem("f_silu_done"), 1)

                def turned(c):
                    for t in range(TT):
                        act.wait_ge(sem("f_turn_ps"), 2 * c + t + 1)
                        nc.scalar.activation(faH[:, t], PS[:, 6 + t, :].rearrange("p (f q) -> p f q", f=4), ACT.Copy)\
                            .then_inc(sem("f_high_done"), 1)

                silu(n0 + 2, 0)
                split_high(act, n0 + 4)
                split_high(act, n0 + 5)
                with act.Fori(0, NC - 1) as i:
                    split_high(act, n0 + 6, i)
                    split_high(act, n0 + 7, i)
                    turned(i)
                    split_high(act, n0 + 8, i)
                    act.wait_ge(sem("f_act_done"), 2 * i + 2)
                    silu(n0 + 6, i)
                    for n in range(9, 12):
                        split_high(act, n0 + n, i)
                turned(NC - 1)

            def deltanet(n0):
                act.dma_start(o_w[:], bcast(b_o_norm[0])).then_inc(loaded_gdn, 16)
                act.dma_start(hpar[:, 0], bcast(b_a_log[0])).then_inc(loaded_gdn, 16)
                act.dma_start(hpar[:, 1], bcast(b_dt_bias[0])).then_inc(loaded_gdn, 16)
                split_high(act, n0)
                split_high(act, n0 + 1)
                norm("gdn")
                turn("gdn", True)
                split_high(act, n0 + 2)

                def first_tap(cb):
                    act.wait_ge(w_used, n0 + 2 * cb + 2)
                    for f in range(4):
                        w = 32 + 24 * (TAPS - 1) + 4 * cb + f
                        last = nc.scalar.activation(cv[:, 4 * cb + f, :], PS[:, 4 * (cb % 2) + f, 0:T], ACT.Copy,
                                                    scale=cols[:, w:w + 1])
                    last.then_inc(sem("tap0_done"), 1)

                def silu(cb):
                    act.wait_ge(sem("taps_done"), cb + 1)
                    nc.scalar.activation(cv[:, 4 * cb:4 * cb + 4, :], cv[:, 4 * cb:4 * cb + 4, :], ACT.Silu)\
                        .then_inc(sem("cv_done"), 1)

                split_high(act, n0 + 3)
                for cb in range(6):
                    split_high(act, n0 + 4 + 2 * cb)
                    first_tap(cb)
                    if cb:
                        silu(cb - 1)
                    if 5 + 2 * cb < 16:
                        split_high(act, n0 + 5 + 2 * cb)
                silu(5)
                for t in range(TT):
                    for cb in range(2):
                        act.wait_ge(w_used, n0 + 14 + 2 * cb)
                        last = nc.scalar.activation(z[:, t, cb * CH:(cb + 1) * CH], PS[:, 4 * cb + t, :], ACT.Silu)
                    last.then_inc(sem("z_done"), 1)
                act.wait_ge(sem("gate_in"), 1)
                link(nc.scalar.activation(t_a[:], t_a[:], ACT.Exp))
                nc.scalar.activation(t_a[:], t_a[:], ACT.Ln, bias=1.0)
                nc.scalar.activation(beta[:], ba_b[:], ACT.Exp, scale=-1.0)
                nc.scalar.activation(nega[:], hpar[:, 0], ACT.Exp).then_inc(sem("gate_exp"), 1)
                for i in range(8):
                    act.wait_ge(sem("tok_ps"), i + 1)
                    a, t, hg = i // 4, i // 2 % 2, i % 2
                    for hh in range(4):
                        last = nc.scalar.activation(tok[:, a, t, 4 * hg + hh, :], PS[:, i, 128 * hh:128 * hh + 128], ACT.Square,
                                                    accum_out=ssq[:, a, t, 4 * hg + hh:4 * hg + hh + 1])
                    last.then_inc(sem("ssq_done"), 1)
                act.wait_ge(sem("gcum_ps"), 1)
                gp = PS[:, 4, 0:64].rearrange("p (a t h) -> p a t h", a=4, t=TT)
                nc.scalar.activation(gcum[:], gp[:, 0], ACT.Copy)
                nc.scalar.activation(egl[:], gp[:, 2:4], ACT.Exp)
                nc.scalar.activation(egc[:], gp[:, 0], ACT.Exp).then_inc(sem("gcum_done"), 1)
                act.wait_ge(sem("kdec_in"), 1)
                nc.scalar.activation(kdec[:], kdec[:], ACT.Exp).then_inc(sem("kdec_done"), 1)
                two = lambda b: PS[:, b:b + 2, :].rearrange("p b (n q) -> p (b n) q", q=128)
                for t in range(TT):
                    act.wait_ge(sem("qkTt_ps"), 2 * t + 1)
                    nc.scalar.activation(qT[:], two(0), ACT.Copy)
                    nc.scalar.activation(kT[:], two(2), ACT.Copy).then_inc(sem("qkTt_done"), 1)
                    act.wait_ge(sem("qkTt_ps"), 2 * t + 2)
                    nc.scalar.activation(qgT[:], two(4), ACT.Copy).then_inc(sem("qkTt_done"), 1)
                    act.wait_ge(sem("decay_in"), t + 1)
                    nc.scalar.activation(decay[:], decay[:], ACT.Exp)
                    nc.scalar.activation(decayT[:], decayT[:], ACT.Exp).then_inc(sem("decay_done"), 1)
                    for l in range(1, LEVELS):
                        for hg in range(2):
                            act.wait_ge(sem("y_ps"), 2 * ((LEVELS - 1) * t + l - 1) + hg + 1)
                            if l >= 2:
                                act.wait_ge(sem("p_ps"), 2 * ((LEVELS - 1) * t + l - 2) + hg + 1)
                            nc.scalar.activation(yT[:, 4 * hg:4 * hg + 4, :], PS[:, hg, :].rearrange("p (n q) -> p n q", n=4),
                                                 ACT.Copy).then_inc(sem("y_done"), 1)
                    act.wait_ge(sem("uw_ps"), t + 1)
                    nc.scalar.activation(u_sol[:], two(0), ACT.Copy)
                    nc.scalar.activation(wT[:], two(2), ACT.Copy).then_inc(sem("uw_done"), 1)
                    act.wait_ge(sem("o_ps"), 2 * t + 2)
                    for hh in range(BH):
                        last = nc.scalar.activation(yT[:, hh, :], two(6)[:, hh, :], ACT.Square, accum_out=sso[:, t, hh:hh + 1])
                    last.then_inc(sem("sso_done"), 1)
                turn("gdn_o", False)
                for n in range(16, 20):
                    split_high(act, n0 + n)

            def experts(n0):
                split_high(act, n0)
                split_high(act, n0 + 1)
                norm("moe")
                turn("moe", True)
                act.wait_ge(xs_done, 2 * (norm_no["moe"] + 1))
                nc.scalar.activation(xsH[:], xs[:], ACT.Copy).then_inc(sem("xsH_done"), 1)
                act.wait_ge(sem("gap_done"), 1)
                nc.scalar.activation(w1[:], gap[:], ACT.Exp).then_inc(sem("gap_exp"), 1)

                def gathered(j):
                    act.wait_ge(sem("gather_ps"), j + 1)
                    for k in range(KD):
                        last = nc.scalar.activation(xH[:, k, 0:128], PS[:, 5 + k // 4, 128 * (k % 4):128 * (k % 4) + 128],
                                                    ACT.Copy, scale=cols[:, 24 + k:25 + k])
                    last.then_inc(sem("gather_high"), 1)

                gathered(0)
                act.wait_ge(sem("jobs_done"), 1)
                njobs = act.value_load(jobs[0:1, NJ:NJ + 1], min_val=E, max_val=JOBS)
                with act.Fori(0, JOBS) as j:
                    with act.If(j < njobs):
                        def silu(n, r):
                            act.wait_ge(w_used, n + r * RAW)
                            nc.scalar.activation(mg[:], PS[:, 0, :], ACT.Silu).then_inc(sem("m_silu_done"), 1)

                        def turned(c):
                            act.wait_ge(sem("m_turn_ps"), j * NC + c + 1)
                            nc.scalar.activation(maH[:], PS[:, 4, :].rearrange("p (f q) -> p f q", f=4), ACT.Copy)\
                                .then_inc(sem("m_high_done"), 1)

                        r0 = j * NC
                        split_high(act, n0 + 2, r0)
                        split_high(act, n0 + 3, r0)
                        silu(n0 + 2, r0)
                        split_high(act, n0 + 4, r0)
                        split_high(act, n0 + 5, r0)
                        with act.Fori(0, NC - 1) as i:
                            r = j * NC + i
                            split_high(act, n0 + 6, r)
                            split_high(act, n0 + 7, r)
                            turned(i)
                            split_high(act, n0 + 8, r)
                            act.wait_ge(sem("m_act_done"), j * NC + i + 1)
                            silu(n0 + 6, r)
                            for n in range(9, 12):
                                split_high(act, n0 + n, r)
                        turned(NC - 1)
                        gathered(j + 1)
                        with act.If(j + 1 < njobs):
                            split_high(act, n0 + SUBS_FFN, r0)
                            split_high(act, n0 + SUBS_FFN + 1, r0)
                        act.wait_ge(sem("back_ps"), j + 1)
                        act.wait_ge(w_used, n0 + SUBS_FFN + r0 * RAW)
                        nc.scalar.activation(ysH[:].rearrange("p (b n) -> p b n", b=2), PS[:, 2:4, :], ACT.Copy)\
                            .then_inc(sem("ys_high"), 1)

            if "att" in stages:
                attention(base["att"])
            if "ffn" in stages:
                ffn(base["ffn"])
            if "gdn" in stages:
                deltanet(base["gdn"])
            if "moe" in stages:
                experts(base["moe"])
            norm("fin")

        @block.tensor
        def _(pe):
            pe.wait_ge(sem("rows_in"), 80)
            pe.wait_ge(sem("ident_in"), 16)
            nc.tensor.transpose(PS[:, 0, 0:128], rows[:], ident).then_inc(sem("cols_ps"), 1)

            def turn(name, src, ready, value):
                m = turn_no[name]
                pe.wait_ge(ready, value)
                for b in range(4):
                    for kk in range(2):
                        for t in range(TT):
                            k = 2 * b + kk
                            last = nc.tensor.transpose(PS[:, 4 + b, 256 * kk + 128 * t:256 * kk + 128 * t + 128],
                                                       src[:, t, 128 * k:128 * k + 128], ident)
                    last.then_inc(xt_ps, 1)

            def x_ready(name, k):
                pe.wait_ge(xl_done, 4 * turn_no[name] + k // 2 + 1)

            def tokens_by_columns(name, n, bank, cb):
                for half in range(2):
                    pe.wait_ge(lo_done, n + half + 1)
                    wh, wl = high_low(n + half, 4)
                    for t in range(TT):
                        for kk in range(4):
                            k = 4 * half + kk
                            if cb == 0 and t == 0:
                                x_ready(name, k)
                            last = mm3(PS[:, bank + t, :], xH[:, k, 128 * t:128 * t + 128], xL[:, k, 128 * t:128 * t + 128],
                                       wh[:, kk], wl[:, kk], k == 0, k == KD - 1)
                    last.then_inc(w_used, 1)

            def attention(n0):
                turn("att", xs, xs_done, 2 * (norm_no["att"] + 1))
                def turn_qk(g):
                    pe.wait_ge(sem("rot_done"), g // 2 + 1)
                    if g >= 4:
                        pe.wait_ge(sem("qkT_done"), g - 3)
                    for i in range(2):
                        for t in range(TT):
                            b = 2 * g + i
                            last = nc.tensor.transpose(PS[:, 4 + g % 4, 256 * i + 128 * t:256 * i + 128 * t + 128],
                                                       rot[:, t, 128 * b:128 * b + 128], ident)
                    last.then_inc(sem("qkT_ps"), 1)

                for cb in range(3):
                    if cb == 2:
                        turn_qk(0)
                        turn_qk(1)
                        pe.wait_ge(sem("qkv_done"), 2)
                    tokens_by_columns("att", n0 + 2 * cb, 2 * (cb % 2), cb)
                for g in range(2, 6):
                    turn_qk(g)

                def scores(a):
                    g, t = a // 2, a % 2
                    for hh in range(AG):
                        hd = AG * g + hh
                        r = slice(64 * (hd % 2), 64 * (hd % 2) + 64)
                        nk = 128 * (t + 1)
                        col = hh // 2 * nk
                        last = nc.tensor.matmul(PS[:, 2 * (a % 2) + hh % 2, col:col + nk],
                                                qkT[r, hd // 2, 128 * t:128 * t + 128], qkT[r, 8 + g, 0:nk],
                                                start=True, stop=True)
                    last.then_inc(sem("score_ps"), 1)

                def turn_probs(a):
                    t = a % 2
                    pe.wait_ge(sem("exp_done"), a + 1)
                    if a:
                        pe.wait_ge(sem("probT_done"), a)
                    for hh in range(AG):
                        for kt in range(t + 1):
                            n = hh * (t + 1) + kt
                            last = nc.tensor.transpose(PS[:, 4 + n // 4, 128 * (n % 4):128 * (n % 4) + 128],
                                                       prob[:, a % 2, hh, 128 * kt:128 * kt + 128], ident)
                    last.then_inc(sem("probT_ps"), 1)

                def values(a):
                    g, t = a // 2, a % 2
                    pe.wait_ge(sem("probT_done"), a + 1)
                    if a >= 2:
                        pe.wait_ge(sem("o_att_done"), a - 1)
                    for hh in range(AG):
                        for kt in range(t + 1):
                            last = nc.tensor.matmul(PS[:, 6 + a % 2, 64 * hh:64 * hh + 64], probT[:, a % 2, hh * (t + 1) + kt, :],
                                                    qkv[:, kt, 1280 + 64 * g:1280 + 64 * g + 64],
                                                    start=(kt == 0), stop=(kt == t))
                    last.then_inc(sem("pv_ps"), 1)

                pe.wait_ge(sem("qkT_done"), 6)
                pe.wait_ge(sem("v_done"), 1)
                scores(0)
                scores(1)
                for a in range(8):
                    turn_probs(a)
                    if a + 2 < 8:
                        pe.wait_ge(sem("masked"), a + 1)
                        scores(a + 2)
                    values(a)
                turn("att_o", o_att, sem("o_att_done"), 8)
                for cb in range(2):
                    tokens_by_columns("att_o", n0 + 6 + 2 * cb, 2 * cb, cb)

            def ffn(n0):
                turn("ffn", xs, xs_done, 2 * (norm_no["ffn"] + 1))

                def gate_up(n, r, bank, free, value, first):
                    for half in range(2):
                        pe.wait_ge(lo_done, n + half + 1 + r * RAW)
                        if half == 0 and free is not None:
                            pe.wait_ge(free, value)
                        wh, wl = high_low(n + half, 4)
                        for t in range(TT):
                            for kk in range(4):
                                k = 4 * half + kk
                                if first and t == 0:
                                    x_ready("ffn", k)
                                last = mm3(PS[:, bank + t, :], xH[:, k, 128 * t:128 * t + 128],
                                           xL[:, k, 128 * t:128 * t + 128], wh[:, kk], wl[:, kk], k == 0, k == KD - 1)
                        last.then_inc(w_used, 1)

                def turned(c):
                    pe.wait_ge(sem("f_y_free"), c + 1)
                    for t in range(TT):
                        pe.wait_ge(sem("f_act_done"), 2 * c + t + 1)
                        for f in range(4):
                            last = nc.tensor.transpose(PS[:, 6 + t, 128 * f:128 * f + 128], fa[:, t, 128 * f:128 * f + 128], ident)
                        last.then_inc(sem("f_turn_ps"), 1)

                def down(n, r, c):
                    for half in range(2):
                        pe.wait_ge(lo_done, n + half + 1 + r * RAW)
                        wh, wl = high_low(n + half, 2)
                        for t in range(TT):
                            if half == 0:
                                pe.wait_ge(sem("f_low_done"), 2 * c + t + 1)
                            for ff in range(2):
                                f = 2 * half + ff
                                for b in range(2):
                                    last = mm3(PS[:, 4 + 2 * t + b, :], faH[:, t, f, :], faL[:, t, f, :],
                                               wh[:, ff, CH * b:CH * b + CH], wl[:, ff, CH * b:CH * b + CH], f == 0, f == 3)
                        last.then_inc(w_used, 1)

                gate_up(n0, 0, 0, None, 0, True)
                gate_up(n0 + 2, 0, 2, None, 0, False)
                with pe.Fori(0, NC - 1) as i:
                    gate_up(n0 + 4, i, 0, sem("f_silu_done"), 2 * i + 2, False)
                    turned(i)
                    gate_up(n0 + 6, i, 2, sem("f_act_done"), 2 * i + 2, False)
                    down(n0 + 8, i, i)
                turned(NC - 1)
                down(n0 + SUBS_FFN - 2, 0, NC - 1)

            def deltanet(n0):
                turn("gdn", xs, xs_done, 2 * (norm_no["gdn"] + 1))
                for cb in range(6):
                    if cb >= 2:
                        pe.wait_ge(sem("taps_done"), cb - 1)
                    for half in range(2):
                        n = n0 + 2 * cb + half
                        pe.wait_ge(lo_done, n + 1)
                        wh, wl = high_low(n, 4)
                        for f in range(4):
                            for kk in range(4):
                                k = 4 * half + kk
                                if cb == 0:
                                    x_ready("gdn", k)
                                c = slice(128 * f, 128 * f + 128)
                                last = mm3(PS[:, 4 * (cb % 2) + f, 0:T], wh[:, kk, c], wl[:, kk, c], xH[:, k, :], xL[:, k, :],
                                           k == 0, k == KD - 1)
                        last.then_inc(w_used, 1)
                for cb in range(2):
                    pe.wait_ge(sem("taps_done"), 5 + cb)
                    tokens_by_columns("gdn", n0 + 12 + 2 * cb, 4 * cb, 1)
                pe.wait_ge(sem("swL_done"), 1)
                for t in range(TT):
                    for k in range(KD):
                        last = mm3(PS[:, 2, 16 * t:16 * t + 16], xH[:, k, 128 * t:128 * t + 128], xL[:, k, 128 * t:128 * t + 128],
                                   swH[:, k, 0:16], swL[:, k, 0:16], k == 0, k == KD - 1)
                last.then_inc(sem("ba_ps"), 1)
                pe.wait_ge(sem("ba_read"), 1)
                pe.wait_ge(sem("z_done"), 2)
                for i in range(12):
                    a, t, hg = i // 4, i // 2 % 2, i % 2
                    pe.wait_ge(sem("cv_done"), 2 * a + hg + 1)
                    if i >= 8:
                        pe.wait_ge(sem("tok_done"), i - 7)
                    for hh in range(4):
                        last = nc.tensor.transpose(PS[:, i % 8, 128 * hh:128 * hh + 128],
                                                   cv[:, 8 * a + 4 * hg + hh, 128 * t:128 * t + 128], ident)
                    last.then_inc(sem("tok_ps"), 1)
                pe.wait_ge(sem("gate_done"), 1)
                pe.wait_ge(sem("tok_done"), 12)
                for i, m in enumerate(("tri", "same", "first", "second")):
                    last = nc.tensor.matmul(PS[:, 4, 16 * i:16 * i + 16], C(m), gate[:].rearrange("p t h -> p (t h)"),
                                            start=True, stop=True)
                last.then_inc(sem("gcum_ps"), 1)

                for t in range(TT):
                    def heads(bank, make):
                        for hh in range(BH):
                            last = make(PS[:, bank + hh // 4, 128 * (hh % 4):128 * (hh % 4) + 128], hh)
                        return last

                    if t:
                        pe.wait_ge(sem("state_done"), 2 * t)
                        pe.wait_ge(sem("o_read"), t)
                    heads(0, lambda o, hh: nc.tensor.transpose(o, q_tok[:, t, hh, :], ident))
                    heads(2, lambda o, hh: nc.tensor.transpose(o, k_tok[:, t, hh, :], ident)).then_inc(sem("qkTt_ps"), 1)
                    pe.wait_ge(sem("gbc_done"), t + 1)
                    if t == 0:
                        pe.wait_ge(sem("gcum_done"), 1)
                    heads(6, lambda o, hh: nc.tensor.matmul(o, yT[:, hh, :], C("tri"), start=True, stop=True))\
                        .then_inc(sem("gb_ps"), 1)
                    pe.wait_ge(sem("qg_done"), t + 1)
                    heads(4, lambda o, hh: nc.tensor.transpose(o, q_tok[:, t, hh, :], ident)).then_inc(sem("qkTt_ps"), 1)
                    pe.wait_ge(sem("qkTt_done"), 2 * t + 1)
                    heads(0, lambda o, hh: nc.tensor.matmul(o, kT[:, hh, :], kT[:, hh, :], start=True, stop=True))
                    heads(2, lambda o, hh: nc.tensor.matmul(o, kT[:, hh, :], qT[:, hh, :], start=True, stop=True))\
                        .then_inc(sem("kk_ps"), 1)
                    pe.wait_ge(sem("lowM0_done"), t + 1)
                    pe.wait_ge(sem("qkTt_done"), 2 * t + 2)
                    heads(4, lambda o, hh: nc.tensor.transpose(o, yT[:, hh, :], ident)).then_inc(sem("lowT_ps"), 1)
                    for l in range(1, LEVELS):
                        n = (LEVELS - 1) * t + l - 1
                        pe.wait_ge(sem("lowM_done"), n + 1)
                        for hg in range(2):
                            pe.wait_ge(sem("inv_done"), 2 * (LEVELS * t + l - 1) + hg + 1)
                            for hh in range(4 * hg, 4 * hg + 4):
                                last = nc.tensor.matmul(PS[:, hg, 128 * (hh % 4):128 * (hh % 4) + 128], lowM[:, hh, :], invT[:, hh, :],
                                                        start=True, stop=True)
                            last.then_inc(sem("y_ps"), 1)
                        for hg in range(2):
                            pe.wait_ge(sem("y_done"), 2 * n + hg + 1)
                            for hh in range(4 * hg, 4 * hg + 4):
                                c = slice(128 * (hh % 4), 128 * (hh % 4) + 128)
                                if l < LEVELS - 1:
                                    nc.tensor.matmul(PS[:, 2 + hg, c], yT[:, hh, :], inv[:, hh, :], start=True, stop=True)
                                last = nc.tensor.matmul(PS[:, 4 + hg, c], inv[:, hh, :], yT[:, hh, :], start=True, stop=True)
                            last.then_inc(sem("p_ps"), 1)
                    pe.wait_ge(sem("inv_done"), 2 * LEVELS * (t + 1))
                    pe.wait_ge(sem("kv_done"), t + 1)
                    heads(0, lambda o, hh: nc.tensor.matmul(o, invT[:, hh, :], vbeta[:, hh, :], start=True, stop=True))
                    heads(2, lambda o, hh: nc.tensor.matmul(o, kbeta[:, hh, :], invT[:, hh, :], start=True, stop=True))\
                        .then_inc(sem("uw_ps"), 1)
                    pe.wait_ge(sem("uw_done"), t + 1)
                    for c in range(2):
                        g = 2 * t + c
                        R = slice(64 * c, 64 * c + 64)
                        S = state[g % 2]
                        if g:
                            pe.wait_ge(sem("state_done"), g)
                            for hh in range(BH):
                                last = nc.tensor.matmul(PS[R, 4 + hh // 4, 128 * (hh % 4):128 * (hh % 4) + 128], wT[:, hh, R], S[:, hh, :],
                                                        start=True, stop=True)
                            last.then_inc(sem("ws_ps"), 1)
                        pe.wait_ge(sem("v_new_done"), g + 1)
                        for hh in range(BH if g < 2 * TT - 1 else 0):
                            last = nc.tensor.matmul(PS[:, hh // 4, 128 * (hh % 4):128 * (hh % 4) + 128], k_tok[R, t, hh, :], v_new[R, hh, :],
                                                    start=True, stop=True)
                        if g < 2 * TT - 1:
                            last.then_inc(sem("ds_ps"), 1)
                        for hh in range(BH):
                            o = PS[R, 6 + hh // 4, 128 * (hh % 4):128 * (hh % 4) + 128]
                            if g:
                                nc.tensor.matmul(o, qgT[:, hh, R], S[:, hh, :], start=True, stop=False)
                            last = nc.tensor.matmul(o, attnT[R, hh, R], v_new[R, hh, :], start=(g == 0), stop=True)
                        last.then_inc(sem("o_ps"), 1)
                turn("gdn_o", z, sem("o_read"), TT)
                for cb in range(2):
                    tokens_by_columns("gdn_o", n0 + 16 + 2 * cb, 2 * cb, cb)

            def experts(n0):
                turn("moe", xs, xs_done, 2 * (norm_no["moe"] + 1))
                pe.wait_ge(sem("swL_done"), 1)
                for t in range(TT):
                    for k in range(KD):
                        x_ready("moe", k)
                        last = mm3(PS[:, 0, E * t:E * t + E], xH[:, k, 128 * t:128 * t + 128], xL[:, k, 128 * t:128 * t + 128],
                                   swH[:, k, 16:16 + E], swL[:, k, 16:16 + E], k == 0, k == KD - 1)
                last.then_inc(sem("logit_ps"), 1)
                pe.wait_ge(sem("sel_done"), 1)
                nc.tensor.matmul(PS[:, 1, 0:E], C("before"), sel[:, 0], start=True, stop=True)
                nc.tensor.matmul(PS[:, 1, E:2 * E], C("ones"), sel[:, 0], start=True, stop=False)
                nc.tensor.matmul(PS[:, 1, E:2 * E], C("before"), sel[:, 1], start=False, stop=True)
                nc.tensor.matmul(PS[:, 1, 2 * E:3 * E], C("ones"), sel[:, 0], start=True, stop=False)
                nc.tensor.matmul(PS[:, 1, 2 * E:3 * E], C("ones"), sel[:, 1], start=False, stop=True).then_inc(sem("place_ps"), 1)

                def gather(j):
                    pe.wait_ge(sem("pick_done"), j + 1)
                    for k in range(KD):
                        o = PS[:, 5 + k // 4, 128 * (k % 4):128 * (k % 4) + 128]
                        for t in range(TT):
                            c = slice(128 * k, 128 * k + 128)
                            nc.tensor.matmul(o, xsH[:, t, c], pick[:, t, :], start=(t == 0), stop=False)
                            last = nc.tensor.matmul(o, xsL[:, t, c], pick[:, t, :], start=False, stop=(t == TT - 1))
                    last.then_inc(sem("gather_ps"), 1)

                def gate_up(n, r, bank):
                    for half in range(2):
                        pe.wait_ge(lo_done, n + half + 1 + r * RAW)
                        wh, wl = high_low(n + half, 4)
                        for kk in range(4):
                            k = 4 * half + kk
                            last = mm3(PS[:, bank, :], xH[:, k, 0:128], xL[:, k, 0:128], wh[:, kk], wl[:, kk], k == 0, k == KD - 1)
                        if half == 0:
                            last.then_inc(w_used, 1)
                    return last

                def turned():
                    for f in range(4):
                        last = nc.tensor.transpose(PS[:, 4, 128 * f:128 * f + 128], ma[:, 128 * f:128 * f + 128], ident)
                    last.then_inc(sem("m_turn_ps"), 1)

                def down(n, r, first, last_chunk):
                    for half in range(2):
                        pe.wait_ge(lo_done, n + half + 1 + r * RAW)
                        wh, wl = high_low(n + half, 2)
                        for ff in range(2):
                            f = 2 * half + ff
                            for b in range(2):
                                last = mm3(PS[:, 2 + b, :], maH[:, f, :], maL[:, f, :], wh[:, ff, CH * b:CH * b + CH],
                                           wl[:, ff, CH * b:CH * b + CH], first and f == 0, last_chunk and f == 3)
                        last.then_inc(w_used, 1)
                    return last

                def back(j):
                    pe.wait_ge(sem("ys_low"), j + 1)
                    for t in range(TT):
                        for b in range(2):
                            o = PS[:, 4 + 2 * t + b, :]
                            nc.tensor.matmul(o, pickT[:, t, :], ysH[:, CH * b:CH * b + CH], start=True, stop=False)
                            last = nc.tensor.matmul(o, pickT[:, t, :], ysL[:, CH * b:CH * b + CH], start=False, stop=True)
                    last.then_inc(sem("back_ps"), 1)

                gather(0)
                pe.wait_ge(sem("jobs_done"), 1)
                njobs = pe.value_load(jobs[0:1, NJ:NJ + 1], min_val=E, max_val=JOBS)
                with pe.Fori(0, JOBS) as j:
                    with pe.If(j < njobs):
                        def gate(n, r):
                            gate_up(n, r, 0).then_inc(w_used, 1)

                        def up(n, r):
                            gate_up(n, r, 1).then_inc(w_used, 1)

                        r0 = j * NC
                        pe.wait_ge(sem("gather_low"), j + 1)
                        gate(n0, r0)
                        back(j)
                        for t in range(TT):
                            last = nc.tensor.matmul(PS[:, 1, 128 * t:128 * t + 128], pick[:, t, :], identR[:], start=True, stop=True)
                        last.then_inc(sem("pickT_ps"), 1)
                        pe.wait_ge(sem("pickT_done"), j + 2)
                        up(n0 + 2, r0)
                        def chunk(i, r, first):
                            pe.wait_ge(sem("m_silu_done"), j * NC + i + 1)
                            gate(n0 + 4, r)
                            if first:
                                pe.wait_ge(sem("added"), j * 4 + 5)
                            pe.wait_ge(sem("m_act_done"), j * NC + i + 1)
                            turned()
                            up(n0 + 6, r)
                            pe.wait_ge(sem("m_low_done"), j * NC + i + 1)
                            down(n0 + 8, r, first, False)

                        chunk(0, r0, True)
                        with pe.Fori(1, NC - 1) as i:
                            chunk(i, j * NC + i, False)
                        pe.wait_ge(sem("m_act_done"), j * NC + NC)
                        turned()
                        gather(j + 1)
                        pe.wait_ge(sem("m_low_done"), j * NC + NC)
                        down(n0 + SUBS_FFN - 2, r0, False, True)
                back(njobs)

            if "att" in stages:
                attention(base["att"])
            if "ffn" in stages:
                ffn(base["ffn"])
            if "gdn" in stages:
                deltanet(base["gdn"])
            if "moe" in stages:
                experts(base["moe"])

        @block.vector
        def _(dve):
            links = [0]

            def link(ins):
                links[0] += 1
                ins.then_inc(sem("dve_link"), 1)
                dve.wait_ge(sem("dve_link"), links[0])

            V = nc.vector
            def norm_columns():
                dve.wait_ge(sem("cols_ps"), 1)
                V.tensor_copy(cols[:], PS[:, 0, 0:128]).then_inc(sem("cols_done"), 1)
                dve.wait_ge(sem("cols_done"), 1)

            def small_low():
                dve.wait_ge(sem("swH_done"), 1)
                V.tensor_tensor(swL[:], small_w[:], swH[:].bitcast(f32), ALU.subtract).then_inc(sem("swL_done"), 1)

            def norm(name):
                n = norm_no[name]
                for t in range(TT):
                    dve.wait_ge(rstd_done, TT * n + t + 1)
                    V.tensor_scalar(xs[:, t], h[:, t], rstd[:, n, t:t + 1], None, ALU.mult).then_inc(xs_done, 1)

            def turn(name, scaled):
                m = turn_no[name]
                for b in range(4):
                    dve.wait_ge(xh_done, 4 * m + b + 1)
                    for kk in range(2):
                        k = 2 * b + kk
                        scale = cols[:, 8 * NORM_COL[name] + k:8 * NORM_COL[name] + k + 1] if scaled else 1.0
                        last = V.scalar_tensor_tensor(out=xL[:, k, :], in0=PS[:, 4 + b, 256 * kk:256 * kk + 256], scalar=scale,
                                                      in1=xH[:, k, :].bitcast(f32), op0=ALU.mult, op1=ALU.subtract)
                    last.then_inc(xl_done, 1)

            def add_to_h(bank, t, cb):
                return V.tensor_tensor(h[:, t, cb * CH:(cb + 1) * CH], PS[:, bank, :], h[:, t, cb * CH:(cb + 1) * CH], ALU.add)

            def project_to_h(name, n, after):
                for cb in range(2):
                    dve.wait_ge(w_used, n + 2 * cb)
                    for t in range(TT):
                        last = add_to_h(2 * cb + t, t, cb)
                        if cb:
                            last.then_inc(h_done, 1)
                    if cb == 0 and stages[-1] != name:
                        split_low(dve, after)
                dve.wait_ge(h_done, TT * (norm_no[name] + 1))

            def attention(n0):
                norm("att")
                norm_columns()
                split_low(dve, n0)
                turn("att", True)
                split_low(dve, n0 + 1)
                split_low(dve, n0 + 2)
                small_low()
                dve.wait_ge(loaded_att, 32)
                dve.wait_ge(sem("cst_in"), 16)
                wide = "p t (h a d) -> p t h a d"
                cos = C("cos").rearrange("p (t d) -> p t d", t=TT)
                sin = C("sin").rearrange("p (t d) -> p t d", t=TT)

                def biased(cb, c0, c1):
                    for t in range(TT):
                        last = V.tensor_tensor(qkv[:, t, cb * CH + c0:cb * CH + c1], PS[:, 2 * (cb % 2) + t, c0:c1],
                                               bias[:, cb * CH + c0:cb * CH + c1], ALU.add)
                    return last

                def rotate(cb, heads):
                    w = heads * AD
                    x4 = qkv[:, :, cb * CH:cb * CH + w]
                    A, B = (r[:, 0:TT * w].rearrange("p (t c) -> p t c", t=TT) for r in (ropeA, ropeB))
                    V.tensor_tensor(A.rearrange("p t (n d) -> p t n d", d=32), x4.rearrange("p t (n d) -> p t n d", d=32),
                                    cos.unsqueeze(2).broadcast_to([128, TT, 2 * heads, 32]), ALU.mult)
                    B5, x5 = B.rearrange(wide, a=2, d=32), x4.rearrange(wide, a=2, d=32)
                    for a in range(2):
                        last = V.tensor_tensor(B5[:, :, :, a, :], x5[:, :, :, 1 - a, :],
                                               sin.unsqueeze(2).broadcast_to([128, TT, heads, 32]), ALU.mult)
                    link(last)
                    A5 = A.rearrange(wide, a=2, d=32)
                    for a, op in ((0, ALU.subtract), (1, ALU.add)):
                        if cb < 2:
                            out5 = rot[:, :, cb * CH:(cb + 1) * CH].rearrange(wide, a=2, d=32)
                            last = V.tensor_tensor(out5[:, :, :, a, :], A5[:, :, :, a, :], B5[:, :, :, a, :], op)
                        else:
                            for twin in range(2):
                                out6 = rot[:, :, 2 * CH:3 * CH].rearrange("p t (h w a d) -> p t h w a d", w=2, a=2, d=32)
                                last = V.tensor_tensor(out6[:, :, :, twin, a, :], A5[:, :, :, a, :], B5[:, :, :, a, :], op)
                    link(last)
                    dve.sem_inc(sem("rot_done"), 1)

                split_low(dve, n0 + 3)
                for cb in range(2):
                    dve.wait_ge(w_used, n0 + 2 * cb + 2)
                    link(biased(cb, 0, CH))
                    dve.sem_inc(sem("qkv_done"), 2)
                    if cb == 0:
                        split_low(dve, n0 + 4)
                    rotate(cb, CH // AD)
                    if cb == 0:
                        split_low(dve, n0 + 5)
                dve.wait_ge(w_used, n0 + 6)
                link(biased(2, 0, AKV * AD))
                rotate(2, AKV)
                biased(2, AKV * AD, CH).then_inc(sem("v_done"), 1)

                def mask(a):
                    g, t = a // 2, a % 2
                    nk = 128 * (t + 1)
                    dve.wait_ge(sem("score_ps"), a + 1)
                    if a >= 2:
                        dve.wait_ge(sem("probT_ps"), a - 1)
                    m = C("att")[:, 256 - nk:256]
                    pairs = prob[:, a % 2, :, 0:nk].rearrange("p (n b) k -> p b n k", b=2)
                    for b in range(2):
                        last = V.scalar_tensor_tensor(out=pairs[:, b], scalar=AD ** -0.5, in1=over_heads(m, 2), op0=ALU.mult, op1=ALU.add,
                                                      in0=PS[:, 2 * (a % 2) + b, 0:2 * nk].rearrange("p (n k) -> p n k", k=nk))
                    link(last)
                    link(V.tensor_reduce(mx[:, a], prob[:, a % 2, :, 0:nk], AX.X, ALU.max))
                    link(V.tensor_tensor(mx[:, a], mx[:, a], sinks[:, AG * g:AG * g + AG], ALU.max))
                    V.tensor_tensor(sink_e[:, a], sinks[:, AG * g:AG * g + AG], mx[:, a], ALU.subtract)
                    V.tensor_scalar(negm[:, a], mx[:, a], -1.0, None, ALU.mult).then_inc(sem("masked"), 1)

                mask(0)
                mask(1)
                split_low(dve, n0 + 6)
                for a in range(8):
                    g, t = a // 2, a % 2
                    dve.wait_ge(sem("exp_done"), a + 1)
                    link(V.tensor_tensor(den[:, a], den[:, a], sink_e[:, a], ALU.add))
                    link(V.reciprocal(rden[:, a], den[:, a]))
                    if a + 2 < 8:
                        mask(a + 2)
                    if a < 2:
                        split_low(dve, n0 + 7 + a)
                    dve.wait_ge(sem("pv_ps"), a + 1)
                    V.tensor_tensor(o_att[:, t, 256 * g:256 * g + 256].rearrange("p (n d) -> p n d", n=AG),
                                    PS[:, 6 + a % 2, 0:256].rearrange("p (n d) -> p n d", n=AG),
                                    per_head(rden[:, a], AD), ALU.mult).then_inc(sem("o_att_done"), 1)
                turn("att_o", False)
                split_low(dve, n0 + 9)
                project_to_h("att", n0 + 8, n0 + 10)

            def ffn(n0):
                norm("ffn")
                turn("ffn", True)
                split_low(dve, n0 + 1)
                split_low(dve, n0 + 2)
                split_low(dve, n0 + 3)
                split_low(dve, n0 + 4)

                def gated(c, n, r):
                    dve.wait_ge(w_used, n + r * RAW)
                    for t in range(TT):
                        dve.wait_ge(sem("f_silu_done"), 2 * c + t + 1)
                        V.tensor_tensor(fa[:, t], PS[:, 2 + t, :], fg[:, t], ALU.mult).then_inc(sem("f_act_done"), 1)

                def turned(c):
                    for t in range(TT):
                        dve.wait_ge(sem("f_high_done"), 2 * c + t + 1)
                        V.tensor_tensor(faL[:, t], PS[:, 6 + t, :].rearrange("p (f q) -> p f q", f=4), faH[:, t].bitcast(f32),
                                        ALU.subtract).then_inc(sem("f_low_done"), 1)

                def add(c, r, n, final=False):
                    dve.wait_ge(w_used, n + r * RAW)
                    dve.wait_ge(sem("f_y_free"), c + 1)
                    for t in range(TT):
                        for b in range(2):
                            last = add_to_h(4 + 2 * t + b, t, b)
                        if final:
                            last.then_inc(h_done, 1)
                    if not final:
                        last.then_inc(sem("f_y_free"), 1)

                dve.sem_inc(sem("f_y_free"), 1)
                gated(0, n0 + 4, 0)
                split_low(dve, n0 + 5)
                with dve.Fori(0, NC - 1) as i:
                    split_low(dve, n0 + 6, i)
                    split_low(dve, n0 + 7, i)
                    turned(i)
                    split_low(dve, n0 + 8, i)
                    split_low(dve, n0 + 9, i)
                    split_low(dve, n0 + 10, i)
                    gated(i + 1, n0 + 8, i)
                    split_low(dve, n0 + 11, i)
                    add(i, i, n0 + 10)
                turned(NC - 1)
                if stages[-1] != "ffn":
                    split_low(dve, n0 + SUBS_FFN)
                add(NC - 1, 0, n0 + SUBS_FFN, True)
                dve.wait_ge(h_done, TT * (norm_no["ffn"] + 1))

            def deltanet(n0):
                norm("gdn")
                turn("gdn", True)
                split_low(dve, n0 + 1)
                split_low(dve, n0 + 2)

                def taps(cb):
                    dve.wait_ge(sem("tap0_done"), cb + 1)
                    for j in range(1, TAPS):
                        for f in range(4):
                            w = 32 + 24 * (TAPS - 1 - j) + 4 * cb + f
                            o = cv[:, 4 * cb + f, j:T]
                            last = V.scalar_tensor_tensor(out=o, in0=PS[:, 4 * (cb % 2) + f, 0:T - j], scalar=cols[:, w:w + 1],
                                                          in1=o, op0=ALU.mult, op1=ALU.add)
                        if j < TAPS - 1:
                            link(last)
                    last.then_inc(sem("taps_done"), 1)

                split_low(dve, n0 + 3)
                for cb in range(6):
                    split_low(dve, n0 + 4 + 2 * cb)
                    taps(cb)
                    if 5 + 2 * cb < 16:
                        split_low(dve, n0 + 5 + 2 * cb)
                dve.wait_ge(sem("ba_ps"), 1)
                dve.wait_ge(loaded_gdn, 48)
                ba = PS[:, 2, 0:32].rearrange("p (t w h) -> p t w h", t=TT, w=2)
                V.tensor_copy(ba_b[:], ba[:, :, 0, :])
                link(V.tensor_tensor(ba_a[:], ba[:, :, 1, :], hpar[:, 1].unsqueeze(1).broadcast_to([128, TT, BH]), ALU.add))
                dve.sem_inc(sem("ba_read"), 1)
                link(V.tensor_scalar(t_b[:], ba_a[:], -1.0, None, ALU.mult))
                V.tensor_tensor(t_a[:], ba_a[:], t_b[:], ALU.min).then_inc(sem("gate_in"), 1)
                dve.wait_ge(sem("gate_exp"), 1)
                V.tensor_scalar(beta[:], beta[:], 1.0, None, ALU.add)
                link(V.scalar_tensor_tensor(out=t_b[:], in0=ba_a[:], scalar=0.0, in1=t_a[:], op0=ALU.max, op1=ALU.add))
                V.scalar_tensor_tensor(out=gate[:], in0=t_b[:], scalar=-1.0, in1=nega[:].unsqueeze(1).broadcast_to([128, TT, BH]),
                                       op0=ALU.mult, op1=ALU.mult)
                V.reciprocal(beta[:], beta[:]).then_inc(sem("gate_done"), 1)
                dve.wait_ge(sem("rq_done"), 1)
                for i in range(12):
                    a, t, hg = i // 4, i // 2 % 2, i % 2
                    o = tok[:, a, t, 4 * hg:4 * hg + 4, :]
                    src = PS[:, i % 8, :].rearrange("p (n d) -> p n d", n=4)
                    dve.wait_ge(sem("tok_ps"), i + 1)
                    if a < 2:
                        V.tensor_tensor(o, src, per_head(rq[:, a, t, 4 * hg:4 * hg + 4], BD), ALU.mult).then_inc(sem("tok_done"), 1)
                    else:
                        V.tensor_copy(o, src).then_inc(sem("tok_done"), 1)
                dve.wait_ge(sem("z_done"), 2)
                z3 = z[:].rearrange("p t (n d) -> p (t n) d", d=BD)
                link(V.tensor_tensor(z3, z3, over_heads(o_w[:], TT * BH), ALU.mult))
                dve.wait_ge(sem("gcum_ps"), 1)
                dve.wait_ge(sem("gcum_done"), 1)
                V.tensor_tensor(kdec[:], PS[:, 4, 16:32].rearrange("p (t h) -> p t h", t=TT), gcum[:], ALU.subtract)\
                    .then_inc(sem("kdec_in"), 1)
                link(V.tensor_tensor(bgc[:], beta[:], egc[:], ALU.mult))
                dve.wait_ge(sem("kdec_done"), 1)
                two = lambda b: PS[:, b:b + 2, :].rearrange("p b (n q) -> p (b n) q", q=128)
                one = lambda b: PS[:, b, :].rearrange("p (n q) -> p n q", q=128)
                for t in range(TT):
                    link(V.tensor_copy(yT[:], per_head(gate[:, t], 128)))
                    dve.sem_inc(sem("gbc_done"), 1)
                    dve.wait_ge(sem("qkTt_ps"), 2 * t + 1)
                    V.tensor_tensor(q_tok[:, t], q_tok[:, t], per_head(egc[:, t], BD), ALU.mult).then_inc(sem("qg_done"), 1)
                    V.tensor_tensor(vbeta[:], v_tok[:, t], per_head(beta[:, t], BD), ALU.mult)
                    link(V.tensor_tensor(kbeta[:], k_tok[:, t], per_head(bgc[:, t], BD), ALU.mult))
                    V.tensor_tensor(k_tok[:, t], k_tok[:, t], per_head(kdec[:, t], BD), ALU.mult).then_inc(sem("kv_done"), 1)
                    dve.wait_ge(sem("gb_ps"), t + 1)
                    V.scalar_tensor_tensor(out=decay[:], in0=two(6), scalar=-1.0, in1=over_heads(C("mask_l"), BH),
                                           op0=ALU.mult, op1=ALU.add)
                    link(V.tensor_tensor(decayT[:], two(6), over_heads(C("mask_t"), BH), ALU.add))
                    V.tensor_tensor(decay[:], decay[:], per_head(gcum[:, t], 128), ALU.add)
                    V.tensor_tensor(decayT[:], decayT[:], per_head(gcum[:, t], 128), ALU.subtract).then_inc(sem("decay_in"), 1)
                    dve.wait_ge(sem("decay_done"), t + 1)
                    dve.wait_ge(sem("kk_ps"), t + 1)
                    link(V.tensor_tensor(low[:], two(0), decay[:], ALU.mult))
                    link(V.tensor_tensor(low[:], low[:], per_head(beta[:, t], 128), ALU.mult))
                    dve.sem_inc(sem("low_done"), 1)
                    link(V.tensor_tensor(yT[:], low[:], over_heads(level[:, 0], BH), ALU.mult))
                    dve.sem_inc(sem("lowM0_done"), 1)
                    V.tensor_tensor(attnT[:], two(2), decayT[:], ALU.mult)
                    V.scalar_tensor_tensor(out=inv[:], in0=yT[:], scalar=-1.0, in1=over_heads(ident, BH), op0=ALU.mult, op1=ALU.add)
                    dve.wait_ge(sem("lowT_ps"), t + 1)
                    for hg in range(2):
                        V.scalar_tensor_tensor(out=invT[:, 4 * hg:4 * hg + 4, :], in0=one(4 + hg), scalar=-1.0,
                                               in1=over_heads(ident, 4), op0=ALU.mult, op1=ALU.add).then_inc(sem("inv_done"), 1)
                    for l in range(1, LEVELS):
                        for hg in range(2):
                            n = 2 * ((LEVELS - 1) * t + l - 1) + hg
                            hs = slice(4 * hg, 4 * hg + 4)
                            dve.wait_ge(sem("p_ps"), n + 1)
                            dve.wait_ge(sem("inv_done"), 2 * (LEVELS * t + l - 1) + hg + 1)
                            if l < LEVELS - 1:
                                V.tensor_tensor(inv[:, hs, :], inv[:, hs, :], one(2 + hg), ALU.subtract)
                            V.tensor_tensor(invT[:, hs, :], invT[:, hs, :], one(4 + hg), ALU.subtract).then_inc(sem("inv_done"), 1)
                    dve.wait_ge(sem("uw_done"), t + 1)
                    for c in range(2):
                        g = 2 * t + c
                        R = slice(64 * c, 64 * c + 64)
                        if g == 0:
                            V.tensor_copy(v_new[R], u_sol[R]).then_inc(sem("v_new_done"), 1)
                            dve.wait_ge(sem("ds_ps"), 1)
                            V.tensor_copy(state[1][:], two(0)).then_inc(sem("state_done"), 1)
                            continue
                        S, Snew = state[g % 2], state[(g + 1) % 2]
                        dve.wait_ge(sem("ws_ps"), g)
                        if g >= 2:
                            dve.wait_ge(sem("o_ps"), g - 1)
                        V.tensor_tensor(v_new[R], u_sol[R], two(4)[R], ALU.subtract).then_inc(sem("v_new_done"), 1)
                        if g < 2 * TT - 1:
                            dve.wait_ge(sem("state_done"), g)
                            dve.wait_ge(sem("o_ps"), g)
                            link(V.tensor_tensor(Snew[:], S[:], per_head(egl[:, c, t], BD), ALU.mult))
                            dve.wait_ge(sem("ds_ps"), g + 1)
                            V.tensor_tensor(Snew[:], Snew[:], two(0), ALU.add).then_inc(sem("state_done"), 1)
                    dve.wait_ge(sem("rso_done"), t + 1)
                    dve.wait_ge(sem("o_ps"), 2 * t + 2)
                    link(V.tensor_tensor(attnT[:], two(6), per_head(rso[:, t], BD), ALU.mult))
                    zt = z[:, t].rearrange("p (n d) -> p n d", d=BD)
                    V.tensor_tensor(zt, zt, attnT[:], ALU.mult).then_inc(sem("o_read"), 1)
                turn("gdn_o", False)
                for n in range(16, 20):
                    split_low(dve, n0 + n)
                project_to_h("gdn", n0 + 18, n0 + 20)

            def experts(n0):
                norm("moe")
                turn("moe", True)
                split_low(dve, n0 + 1)
                V.tensor_copy(identR[:], ident)
                dve.wait_ge(sem("xsH_done"), 1)
                V.tensor_tensor(xsL[:], xs[:], xsH[:].bitcast(f32), ALU.subtract)
                iota8 = C("iota")[:, 0:E]

                def picks(e, shift):
                    for t in range(TT):
                        last = V.tensor_scalar(pick[:, t], C("iota")[:, shift] if isinstance(shift, slice)
                                               else cst[:, ds(shift + CONST["iota"][0], 128)],
                                               key[:, t, ds(e, 1)] if not isinstance(e, int) else key[:, t, e:e + 1],
                                               None, ALU.is_equal)
                    last.then_inc(sem("pick_done"), 1)

                dve.wait_ge(sem("logit_ps"), 1)
                link(V.tensor_copy(lg[:], PS[:, 0, 0:2 * E].rearrange("p (t e) -> p t e", t=TT)))
                for t in range(TT):
                    link(V.max(top[:, t], lg[:, t]))
                    link(V.max_index(topi[:, t], top[:, t], lg[:, t]))
                link(V.tensor_copy(topf[:], topi[:]))
                for t in range(TT):
                    V.tensor_scalar(sel0[:, t], iota8, topf[:, t, 0:1], None, ALU.is_equal)
                    V.tensor_scalar(sel1[:, t], iota8, topf[:, t, 1:2], None, ALU.is_equal)
                link(V.tensor_tensor(gap[:], top[:, :, 1], top[:, :, 0], ALU.subtract))
                dve.sem_inc(sem("gap_done"), 1)
                link(V.tensor_tensor(sel[:], sel0[:], sel1[:], ALU.add))
                dve.sem_inc(sem("sel_done"), 1)
                dve.wait_ge(sem("place_ps"), 1)
                link(V.scalar_tensor_tensor(out=key[:], in0=PS[:, 1, 0:2 * E].rearrange("p (t e) -> p t e", t=TT), scalar=1.0,
                                            in1=sel[:], op0=ALU.add, op1=ALU.mult))
                link(V.tensor_scalar(key[:], key[:], -1.0, None, ALU.add))
                picks(0, slice(0, 128))
                link(V.tensor_scalar(over[:], PS[:, 1, 2 * E:3 * E], 128.5, None, ALU.is_gt))
                link(V.memset(opos[:], 0.0))
                for e in range(1, E):
                    link(V.tensor_tensor(opos[:, e:e + 1], opos[:, e - 1:e], over[:, e - 1:e], ALU.add))
                link(V.memset(jobf[:], 0.0))
                V.tensor_copy(jobf[:, 1:E + 1], iota8)
                link(V.tensor_tensor(jobf[:, NJ:NJ + 1], opos[:, E - 1:E], over[:, E - 1:E], ALU.add))
                link(V.tensor_scalar(jobf[:, NJ:NJ + 1], jobf[:, NJ:NJ + 1], float(E), None, ALU.add))
                for k in range(JOBS - E):
                    link(V.scalar_tensor_tensor(out=hit[:], in0=opos[:], scalar=float(k), in1=over[:], op0=ALU.is_equal, op1=ALU.mult))
                    link(V.tensor_tensor(hit[:], hit[:], iota8, ALU.mult))
                    link(V.tensor_reduce(jobf[:, E + k + 1:E + k + 2], hit[:], AX.X, ALU.add))
                link(V.tensor_copy(jobs[:], jobf[:]))
                dve.sem_inc(sem("jobs_done"), 1)

                def gathered(j):
                    dve.wait_ge(sem("gather_high"), j + 1)
                    for k in range(KD):
                        last = V.scalar_tensor_tensor(out=xL[:, k, 0:128], in0=PS[:, 5 + k // 4, 128 * (k % 4):128 * (k % 4) + 128],
                                                      scalar=cols[:, 24 + k:25 + k], in1=xH[:, k, 0:128].bitcast(f32),
                                                      op0=ALU.mult, op1=ALU.subtract)
                    last.then_inc(sem("gather_low"), 1)

                gathered(0)
                dve.wait_ge(sem("gap_exp"), 1)
                link(V.tensor_scalar(w0[:], w1[:], 1.0, None, ALU.add))
                link(V.reciprocal(w0[:], w0[:]))
                link(V.tensor_tensor(w1[:], w1[:], w0[:], ALU.mult))
                for t in range(TT):
                    link(V.tensor_scalar(cw[:, t], sel0[:, t], w0[:, t:t + 1], None, ALU.mult))
                    link(V.scalar_tensor_tensor(out=cw[:, t], in0=sel1[:, t], scalar=w1[:, t:t + 1], in1=cw[:, t],
                                                op0=ALU.mult, op1=ALU.add))
                V.memset(ysH[:].bitcast(f32), 0.0)
                V.memset(ysL[:].bitcast(f32), 0.0)
                V.memset(pickT[:].bitcast(f32), 0.0).then_inc(sem("pickT_done"), 1)
                dve.wait_ge(sem("pickT_done"), 1)
                dve.sem_inc(sem("ys_low"), 1)
                dve.sem_inc(sem("added"), 1)

                def add(j, e):
                    dve.wait_ge(sem("back_ps"), j + 1)
                    dve.wait_ge(sem("added"), 4 * j + 1)
                    for t in range(TT):
                        for b in range(2):
                            c = slice(CH * b, CH * b + CH)
                            V.scalar_tensor_tensor(out=h[:, t, c], in0=PS[:, 4 + 2 * t + b, :], scalar=cw[:, t, ds(e, 1)],
                                                   in1=h[:, t, c], op0=ALU.mult, op1=ALU.add).then_inc(sem("added"), 1)

                njobs = dve.value_load(jobs[0:1, NJ:NJ + 1], min_val=E, max_val=JOBS)
                with dve.Fori(0, JOBS) as j:
                    with dve.If(j < njobs):
                        def gated(c, n, r):
                            dve.wait_ge(w_used, n + r * RAW)
                            dve.wait_ge(sem("m_silu_done"), j * NC + c + 1)
                            V.tensor_tensor(ma[:], PS[:, 1, :], mg[:], ALU.mult).then_inc(sem("m_act_done"), 1)

                        def turned(c):
                            dve.wait_ge(sem("m_high_done"), j * NC + c + 1)
                            V.tensor_tensor(maL[:], PS[:, 4, :].rearrange("p (f q) -> p f q", f=4), maH[:].bitcast(f32),
                                            ALU.subtract).then_inc(sem("m_low_done"), 1)

                        r0 = j * NC
                        split_low(dve, n0 + 2, r0)
                        split_low(dve, n0 + 3, r0)
                        dve.wait_ge(sem("pickT_ps"), j + 1)
                        V.tensor_copy(pickT[:], PS[:, 1, 0:256].rearrange("p (t c) -> p t c", t=TT)).then_inc(sem("pickT_done"), 1)
                        prev = dve.value_load(jobs[0:1, ds(j, 1)], min_val=0, max_val=E - 1)
                        add(j, prev)
                        nxt = dve.value_load(jobs[0:1, ds(j + 2, 1)], min_val=0, max_val=E - 1)
                        picks(nxt, ((j + 1) // E) * 128)
                        split_low(dve, n0 + 4, r0)
                        gated(0, n0 + 4, r0)
                        split_low(dve, n0 + 5, r0)
                        with dve.Fori(0, NC - 1) as i:
                            r = j * NC + i
                            split_low(dve, n0 + 6, r)
                            split_low(dve, n0 + 7, r)
                            turned(i)
                            split_low(dve, n0 + 8, r)
                            split_low(dve, n0 + 9, r)
                            gated(i + 1, n0 + 8, r)
                            split_low(dve, n0 + 10, r)
                            split_low(dve, n0 + 11, r)
                        turned(NC - 1)
                        gathered(j + 1)
                        with dve.If(j + 1 < njobs):
                            split_low(dve, n0 + SUBS_FFN, r0)
                            split_low(dve, n0 + SUBS_FFN + 1, r0)
                        dve.wait_ge(sem("ys_high"), j + 1)
                        V.tensor_tensor(ysL[:].rearrange("p (b n) -> p b n", b=2), PS[:, 2:4, :],
                                        ysH[:].bitcast(f32).rearrange("p (b n) -> p b n", b=2), ALU.subtract).then_inc(sem("ys_low"), 1)
                final = dve.value_load(jobs[0:1, ds(njobs, 1)], min_val=0, max_val=E - 1)
                add(njobs, final)
                dve.wait_ge(sem("added"), njobs * 4 + 5)
                dve.sem_inc(h_done, TT)

            if "att" in stages:
                attention(base["att"])
            if "ffn" in stages:
                ffn(base["ffn"])
            if "gdn" in stages:
                deltanet(base["gdn"])
            if "moe" in stages:
                experts(base["moe"])
            n = norm_no["fin"]
            for t in range(TT):
                dve.wait_ge(rstd_done, TT * n + t + 1)
                V.scalar_tensor_tensor(out=fin[:, t], in0=h[:, t], scalar=rstd[:, n, t:t + 1], in1=w_fin[:],
                                       op0=ALU.mult, op1=ALU.mult).then_inc(sem("fin_done"), 1)


_INS = ['x', 'a_norm', 'a_w_qkv', 'a_b_qkv', 'a_sinks', 'a_w_o', 'f_norm', 'f_w_gate', 'f_w_up', 'f_w_down',
        'b_norm', 'b_w_in', 'b_conv_w', 'b_a_log', 'b_dt_bias', 'b_o_norm', 'b_w_o',
        'm_norm', 'm_w_router', 'm_w_gate', 'm_w_up', 'm_w_down', 'final_norm']


def kernel(**inputs):
    import concourse.bacc as _bacc
    from concourse.bass_utils import run_bass_kernel_spmd as _run

    nc = _bacc.Bacc("TRN2", target_bir_lowering=False, num_devices=1)
    arrays, args = {}, []
    for name in _INS:
        a = np.ascontiguousarray(inputs[name])
        arrays[f"in_{name}"] = a
        args.append(nc.dram_tensor(f"in_{name}", a.shape, mybir.dt.from_np(a.dtype), kind="ExternalInput").ap())
    arrays["in_consts"] = constants()
    args.append(nc.dram_tensor("in_consts", (128, NCONST), mybir.dt.float32, kind="ExternalInput").ap())
    out = nc.dram_tensor("out_dram", (1, T, D), mybir.dt.float32, kind="ExternalOutput").ap()
    hybrid_kernel(nc, *args, out)
    r = _run(nc, [arrays], core_ids=[0])
    return r.results[0]["out_dram"]
```
